# Optimizing a Trainium2 kernel written in Bass

```python
import jax, jax.numpy as jnp
from jax import lax
import numpy as np

D_MODEL = 2048
BATCH = 1
SEQ = 256
DEPTH = 1

D_POOL = D_MODEL // 2
POOL_WINDOWS = (2, 4, 8, 16)
POOL_GROUPS = len(POOL_WINDOWS)
POOL_GW = D_POOL // POOL_GROUPS
D_HGRN = D_MODEL // 2
HGRN_HEAD_DIM = 128
HGRN_HEADS = D_HGRN // HGRN_HEAD_DIM
CHUNK = 64
D_IN = D_POOL + 4 * D_HGRN + 2 * D_MODEL
D_FF = ((8 * D_MODEL // 3 + 127) // 128) * 128
CONV_WIDTH = 3
PLE_DIM = 256
EPS = 1e-6

kernel_name = "hybrid_pool_hgrn2_gated_block"

def rms_norm(x, w):
    xf = x.astype(jnp.float32)
    y = xf * lax.rsqrt(jnp.mean(xf * xf, axis=-1, keepdims=True) + EPS)
    return (y * w.astype(jnp.float32)).astype(x.dtype)

def multiscale_pool(u, w_mix, scale):
    B, S, _ = u.shape
    uf = u.astype(jnp.float32)
    cs0 = jnp.concatenate([jnp.zeros((B, 1, D_POOL), jnp.float32), jnp.cumsum(uf, axis=1)], axis=1)
    pos = jnp.arange(1, S + 1, dtype=jnp.float32)
    outs = []
    for g, w in enumerate(POOL_WINDOWS):
        c0 = cs0[..., g * POOL_GW:(g + 1) * POOL_GW]
        upper = c0[:, 1:]
        lower = jnp.concatenate([jnp.zeros((B, w - 1, POOL_GW), jnp.float32), c0[:, :S - w + 1]], axis=1)
        cnt = jnp.minimum(pos, float(w))[None, :, None]
        outs.append((upper - lower) / cnt)
    pooled = jnp.stack(outs, axis=2)
    d = (pooled - uf.reshape(B, S, POOL_GROUPS, POOL_GW)).astype(u.dtype)
    y = jnp.einsum('bsgc,gcd->bsgd', d, w_mix).reshape(B, S, D_POOL)
    return y * scale

def hgrn2(q, f_logit, inp, g, lb, norm_w):
    B, S, _ = q.shape
    H, Dh, C = HGRN_HEADS, HGRN_HEAD_DIM, CHUNK
    N = S // C
    f32 = jnp.float32
    lbf = lb.astype(f32)
    fl = f_logit.astype(f32)
    f = lbf + (1.0 - lbf) * jax.nn.sigmoid(fl)
    log_f = jnp.log(f)
    k = (1.0 - lbf) * jax.nn.sigmoid(-fl)

    def to_chunks(t):
        t = t.astype(f32).reshape(B, N, C, H, Dh)
        return jnp.transpose(t, (1, 0, 3, 2, 4))

    qc, kc, vc = to_chunks(q), to_chunks(k), to_chunks(inp)
    bc = jnp.cumsum(to_chunks(log_f), axis=-2)
    mask = jnp.tril(jnp.ones((C, C), dtype=bool))[:, :, None]

    def step(state, xs):
        q_, k_, v_, b_ = xs
        o_inter = jnp.einsum('bhtk,bhkv->bhtv', q_ * jnp.exp(b_), state)
        diff = b_[:, :, :, None, :] - b_[:, :, None, :, :]
        decay = jnp.exp(jnp.where(mask, diff, -jnp.inf))
        scores = jnp.einsum('bhtk,bhtsk,bhsk->bhts', q_, decay, k_)
        o = o_inter + jnp.einsum('bhts,bhsv->bhtv', scores, v_)
        b_last = b_[:, :, -1:, :]
        new_state = jnp.exp(b_last[:, :, 0, :])[..., None] * state + \
            jnp.einsum('bhsk,bhsv->bhkv', k_ * jnp.exp(b_last - b_), v_)
        return new_state, o

    state0 = jnp.zeros((B, H, Dh, Dh), f32)
    _, o = lax.scan(step, state0, (qc, kc, vc, bc))
    o = jnp.transpose(o, (1, 0, 3, 2, 4)).reshape(B, S, H, Dh)
    o = o * lax.rsqrt(jnp.mean(o * o, axis=-1, keepdims=True) + EPS)
    o = o * norm_w.astype(f32).reshape(H, Dh)
    o = o.reshape(B, S, D_HGRN) * jax.nn.silu(g.astype(f32))
    return o.astype(q.dtype)

def causal_depthwise_conv(z, w, b):
    S = z.shape[1]
    zp = jnp.pad(z, ((0, 0), (CONV_WIDTH - 1, 0), (0, 0)))
    y = b
    for j in range(CONV_WIDTH):
        y = y + w[j] * zp[:, j:j + S]
    return y

def setup_inputs(seed: int = 0) -> dict:
    key = jax.random.key(seed)
    ks = jax.random.split(key, 24)
    f32 = jnp.float32

    def nrm(k, shape, scale):
        return jax.random.normal(k, shape, f32) * scale

    L = DEPTH
    return {
        "x": nrm(ks[0], (BATCH, SEQ, D_MODEL), 1.0),
        "p": nrm(ks[1], (DEPTH, BATCH, SEQ, PLE_DIM), 1.0),
        "ln_mix_w": 1.0 + nrm(ks[2], (L, D_MODEL), 0.02),
        "w_in": nrm(ks[3], (L, D_MODEL, D_IN), D_MODEL ** -0.5),
        "pool_mix_w": nrm(ks[4], (L, POOL_GROUPS, POOL_GW, POOL_GW), POOL_GW ** -0.5),
        "pool_scale": 1.0 + nrm(ks[5], (L, D_POOL), 0.02),
        "hgrn_lb_logits": nrm(ks[6], (DEPTH + 1, D_HGRN), 0.1),
        "hgrn_norm_w": 1.0 + nrm(ks[7], (L, D_HGRN), 0.02),
        "w_branch_a": nrm(ks[8], (L, D_POOL, D_MODEL), D_POOL ** -0.5),
        "w_branch_b": nrm(ks[9], (L, D_HGRN, D_MODEL), D_HGRN ** -0.5),
        "w_out": nrm(ks[10], (L, D_MODEL, D_MODEL), D_MODEL ** -0.5),
        "ln_ffn_w": 1.0 + nrm(ks[11], (L, D_MODEL), 0.02),
        "w_up": nrm(ks[12], (L, D_MODEL, 2 * D_FF), D_MODEL ** -0.5),
        "conv_w": nrm(ks[13], (L, CONV_WIDTH, 2 * D_FF), CONV_WIDTH ** -0.5),
        "conv_b": nrm(ks[14], (L, 2 * D_FF), 0.01),
        "w_down": nrm(ks[15], (L, D_FF, D_MODEL), D_FF ** -0.5),
        "ln_ple_w": 1.0 + nrm(ks[16], (L, D_MODEL), 0.02),
        "w_ple_gate": nrm(ks[17], (L, D_MODEL, D_MODEL), D_MODEL ** -0.5),
        "w_ple": nrm(ks[18], (L, PLE_DIM, D_MODEL), PLE_DIM ** -0.5),
        "ln_final_w": 1.0 + nrm(ks[19], (D_MODEL,), 0.02),
    }

def reference(x, p, ln_mix_w, w_in, pool_mix_w, pool_scale, hgrn_lb_logits, hgrn_norm_w,
              w_branch_a, w_branch_b, w_out, ln_ffn_w, w_up, conv_w, conv_b, w_down,
              ln_ple_w, w_ple_gate, w_ple, ln_final_w):
    lb_all = jnp.cumsum(jax.nn.softmax(hgrn_lb_logits.astype(jnp.float32), axis=0), axis=0)
    split_idx = [D_POOL + j * D_HGRN for j in range(5)] + [D_POOL + 4 * D_HGRN + D_MODEL]
    for i in range(DEPTH):
        h = rms_norm(x, ln_mix_w[i])
        proj = h @ w_in[i]
        u_pool, q, f_logit, inp, g, gate_a, gate_b = jnp.split(proj, split_idx, axis=-1)
        y_a = multiscale_pool(u_pool, pool_mix_w[i], pool_scale[i]) @ w_branch_a[i]
        y_b = hgrn2(q, f_logit, inp, g, lb_all[i], hgrn_norm_w[i]) @ w_branch_b[i]
        merged = jax.nn.sigmoid(gate_a) * y_a + jax.nn.sigmoid(gate_b) * y_b
        x = x + merged @ w_out[i]
        h2 = rms_norm(x, ln_ffn_w[i])
        u = causal_depthwise_conv(h2 @ w_up[i], conv_w[i], conv_b[i])
        u_gate, u_val = jnp.split(u, 2, axis=-1)
        x = x + (jax.nn.silu(u_gate) * u_val) @ w_down[i]
        h3 = rms_norm(x, ln_ple_w[i])
        x = x + jax.nn.sigmoid(h3 @ w_ple_gate[i]) * (p[i] @ w_ple[i])
    return rms_norm(x, ln_final_w)


_drawn_inputs = setup_inputs


def setup_inputs(seed=0):
    import zlib

    import numpy as np

    out = dict(_drawn_inputs(seed))
    spreads = {}
    factors = {'ln_mix_w': 3.473,
     'pool_scale': 59.1,
     'hgrn_norm_w': 78.232,
     'ln_ffn_w': 14.316,
     'conv_b': 27.988,
     'ln_ple_w': 200.0,
     'ln_final_w': 24.504,
     'w_ple_gate': 22.832,
     'p': 8.0,
     'w_ple': 8.0}
    for name, (base, spread) in spreads.items():
        noise = np.random.default_rng([zlib.crc32(name.encode()), seed]).standard_normal(out[name].shape)
        drawn = base * np.exp(spread * noise) if base else spread * noise
        out[name] = __import__('jax').numpy.asarray(drawn.astype(out[name].dtype))
    for name, factor in factors.items():
        out[name] = (out[name] * factor).astype(out[name].dtype)
    return out
```

```python
from contextlib import ExitStack

import concourse.bass as bass
import numpy as np
from concourse import mybir

ALU = mybir.AluOpType
ACT = mybir.ActivationFunctionType
AX_X = mybir.AxisListType.X
F32 = mybir.dt.float32
F32R = mybir.dt.float32r
I32 = mybir.dt.int32

P = 128
SEQ = 256
TB = SEQ // P
D = 2048
KD = D // P
D_POOL = 1024
D_HGRN = 1024
WINDOWS = (2, 4, 8, 16)
GW = D_POOL // len(WINDOWS)
HEADS = 8
CHUNK = 64
D_IN = D_POOL + 4 * D_HGRN + 2 * D
D_FF = ((8 * D // 3 + 127) // 128) * 128
KF = D_FF // P
PLE = 256
EPS = 1e-6
NCOL = 512
NQ = D // NCOL
FW = NCOL // 2
LAST_FW = D_FF % FW
HALVES = (64, 32, 16, 8, 4, 2, 1)
LN_MIN = 2.0 ** -64

RING = 4
LEAD = RING - 1
UK = KD // 2
UB = D_POOL // P // 2
UD = (KF + 1) // 2
NUP = (D_FF + FW - 1) // FW
MIX = 10 * UK
WOUT = MIX + NQ * 2 * (UK + UB)
UP = WOUT + NQ * UK
DOWN = UP + NUP * UK
PLEW = DOWN + NQ * UD
GATE = PLEW + NQ * (PLE // P // 2)
UNITS = GATE + NQ * UK

C_MIX = 10
C_WOUT = C_MIX + 4 * NQ
C_UP = C_WOUT + NQ
C_DOWN = C_UP + NUP
C_PLEW = C_DOWN + NQ
C_GATE = C_PLEW + NQ
COL_Q, COL_F, COL_I, COL_G = (D_POOL + j * D_HGRN for j in range(4))
COL_GA = D_POOL + 4 * D_HGRN
COL_GB = COL_GA + D
PROJ = [c + NCOL * g for g in range(2) for c in (COL_Q, COL_F, COL_I, COL_G)] + [0, NCOL]

END = [UK * (c + 1) for c in range(10)]
LEVEL0 = [END[4 * g + 1] + 5 for g in range(2)]
PV = [LEVEL0[g] + 18 for g in range(2)]
OBT = [PV[g] + 4 for g in range(2)]


def level_slot(g, l):
    return LEVEL0[g] + 2 * (l - 1)


def merge_slot(n, k):
    return MIX + n * 2 * (UK + UB) + (UK, 2 * UK, 2 * UK + UB, 2 * (UK + UB))[k]


def out_slot(n):
    return WOUT + UK * (n + 1)


def up_slot(j):
    return UP + UK * (j + 1)


def down_slot(n):
    return DOWN + UD * (n + 1)


def ple_slot(n):
    return PLEW + n + 1


def gate_slot(n):
    return GATE + UK * (n + 1)


def chunk_end(c):
    if c < C_MIX:
        return END[c]
    if c < C_WOUT:
        return merge_slot((c - C_MIX) // 4, (c - C_MIX) % 4)
    if c < C_UP:
        return out_slot(c - C_WOUT)
    if c < C_DOWN:
        return up_slot(c - C_UP)
    if c < C_PLEW:
        return down_slot(c - C_DOWN)
    return ple_slot(c - C_PLEW) if c < C_GATE else gate_slot(c - C_GATE)


P_T = DOWN + 14

AUX_USES = sorted(
    [(-2, "vec"), (-1, "xT0"), (0, "xT1"), (2, "xT2"), (4, "xT3"), (6, "cvec")]
    + [(END[4 * g] + 1, f"qT{g}") for g in range(2)]
    + [(END[4 * g + 1] + 1, f"fT{g}") for g in range(2)]
    + [(LEVEL0[g] + 1, f"diag{g}") for g in range(2)]
    + [(level_slot(g, l) + 2, f"prod{g}.{l}") for g in range(2) for l in range(1, 9)]
    + [(PV[g], f"pv{g}") for g in range(2)]
    + [(OBT[g], f"obT{g}") for g in range(2)]
    + [(END[8 + g] + 1 + 2 * k, f"{('band', 'mix')[k]}{g}") for g in range(2) for k in range(2)]
    + [(merge_slot(n, 3) + 1, f"mT{n}") for n in range(NQ)]
    + [(out_slot(n) + 1, f"x1T{n}") for n in range(NQ)]
    + [(up_slot(j) + 1, f"zT{j:02d}") for j in range(NUP)]
    + [(P_T, "pT")]
    + [(down_slot(n) + 1, f"x2T{n}") for n in range(NQ)]
)
AUX = {name: a for a, (_, name) in enumerate(AUX_USES)}
AUX_AT = {}
for _slot, _name in AUX_USES:
    AUX_AT.setdefault(_slot, []).append(_name)
assert len(AUX) == len(AUX_USES)

VECS = [("ln_mix", KD), ("ln_ffn", KD), ("ln_ple", KD), ("pool_scale", 8), ("hgrn_norm", 8), ("lb", 16)]
VCOL = {}
_n = 0
for _name, _rows in VECS:
    VCOL[_name] = _n
    _n += _rows
NVEC = _n
UP_PAIRS = (NUP - 2) // 2


def plus(base, per, it):
    return base if it is None else it * per + base


def build(nc, x, p, ln_mix_w, w_in, pool_mix_w, pool_scale, hgrn_lb_logits, hgrn_norm_w, w_branch_a,
          w_branch_b, w_out, ln_ffn_w, w_up, conv_w, conv_b, w_down, ln_ple_w, w_ple_gate, w_ple,
          ln_final_w, ident_c, levels_c, band_c, out):
    with ExitStack() as ctx:
        def sem(name):
            return ctx.enter_context(nc.semaphore(name))

        def sb(name, shape, dt=F32, where=ctx):
            return where.enter_context(nc.sbuf_tensor(name, shape, dt))

        x_tok = sb("x_tok", [P, TB, D])
        xT_hi = sb("xT_hi", [P, KD, SEQ], F32R)
        xT_lo = sb("xT_lo", [P, KD, SEQ], F32R)
        raw = sb("raw", [P, RING, 2, NCOL])
        w_hi = sb("w_hi", [P, RING, 2, NCOL], F32R)
        w_lo = sb("w_lo", [P, RING, 2, NCOL], F32R)
        ident = sb("ident", [P, P])
        vecT = sb("vecT", [P, NVEC])
        convT = sb("convT", [P, 4, 2 * KF])
        lbT = sb("lbT", [P, 2, HEADS])
        ssq = sb("ssq", [P, 4, TB, NQ])
        rstd = sb("rstd", [P, 4, TB])
        st = sb("st", [P, 4, TB])
        minus_half = sb("minus_half", [P, TB * 4])
        nrm = sb("nrm", [P, 4, TB * 4])
        junk = sb("junk", [P, NCOL])
        warm = sb("warm", [P, TB * 4])
        mixer = ExitStack()
        yaT_hi = sb("yaT_hi", [P, 8, SEQ], F32R, mixer)
        yaT_lo = sb("yaT_lo", [P, 8, SEQ], F32R, mixer)
        obT_hi = sb("obT_hi", [P, 8, SEQ], F32R, mixer)
        obT_lo = sb("obT_lo", [P, 8, SEQ], F32R, mixer)
        sig_a = sb("sig_a", [P, TB, NCOL], F32, mixer)
        sig_b = sb("sig_b", [P, TB, NCOL], F32, mixer)
        hg = ExitStack()
        tok = sb("tok", [P, TB, NCOL], F32, hg)
        qT = sb("qT", [P, 4, SEQ], F32, hg)
        kT = sb("kT", [P, 4, SEQ], F32, hg)
        bT = sb("bT", [P, 4, SEQ], F32, hg)
        dec = sb("dec", [P, 2, 4 * SEQ], F32, hg)
        scT = sb("scT", [P, 8, P], F32, hg)
        scX = sb("scX", [P, 4, P], F32, hg)
        v_tok = sb("v_tok", [P, TB, NCOL], F32, hg)
        g_tok = sb("g_tok", [P, TB, NCOL], F32, hg)
        scan_keep = sb("scan_keep", [P, 4 * SEQ], F32, hg)
        levels = sb("levels", [P, len(HALVES), P // 2], F32, hg)
        band = sb("band", [P, 4, 3 * P], F32, hg)
        dT = sb("dT", [P, 4, SEQ], F32, hg)
        mixw = sb("mixw", [P, 4, 2, GW], F32, hg)
        mrows = sb("mrows", [KD, P], F32, hg)
        vrows = sb("vrows", [NVEC - KD, P], F32, hg)
        crows = sb("crows", [2 * KF, 4, P], F32, hg)
        hg.close()
        mg = ExitStack()
        mT_hi = sb("mT_hi", [P, KD, SEQ], F32R, mg)
        mT_lo = sb("mT_lo", [P, KD, SEQ], F32R, mg)
        m_tok = sb("m_tok", [P, TB, NCOL], F32, mg)
        mg.close()
        mixer.close()
        ffn = ExitStack()
        aT_hi = sb("aT_hi", [P, KF, SEQ], F32R, ffn)
        aT_lo = sb("aT_lo", [P, KF, SEQ], F32R, ffn)
        up_tmp = ExitStack()
        z_tok = sb("z_tok", [P, TB, NCOL], F32, up_tmp)
        cv = sb("cv", [P, 4, SEQ], F32, up_tmp)
        act_sig = sb("act_sig", [P, 2, SEQ], F32, up_tmp)
        act = sb("act", [P, 2, SEQ], F32, up_tmp)
        up_tmp.close()
        p_tok = sb("p_tok", [P, TB, PLE], F32, ffn)
        pT_hi = sb("pT_hi", [P, 2, SEQ], F32R, ffn)
        pT_lo = sb("pT_lo", [P, 2, SEQ], F32R, ffn)
        ffn.close()
        last = ExitStack()
        ple_tok = sb("ple_tok", [P, TB, D], F32, last)
        lnf = sb("lnf", [P, D], F32, last)
        sig_g = sb("sig_g", [P, TB, NCOL], F32, last)
        last.close()

        main = ctx.enter_context(nc.psum_tensor("main", [P, 2, TB, NCOL], F32))
        aux = ctx.enter_context(nc.psum_tensor("aux", [P, 2, 2 * NCOL], F32))

        raw_full = [sem(f"raw_full{r}") for r in range(RING)]
        hi_full = sem("hi_full")
        lo_full = sem("lo_full")
        units_done = sem("units_done")
        aux_ready = sem("aux_ready")
        x_in = [sem(f"x_in{n}") for n in range(NQ)]
        const_in, vec_in, late_in, p_in, lnf_in, out_done = map(
            sem, ("const_in", "vec_in", "late_in", "p_in", "lnf_in", "out_done"))
        vec_ready, cvec_ready, lb_ready, scan_keep_set, half_set = map(
            sem, ("vec_ready", "cvec_ready", "lb_ready", "scan_keep_set", "half_set"))
        xT_hi_ready, xT_ready = map(sem, ("xT_hi_ready", "xT_ready"))
        tok_ready = sem("tok_ready")
        qT_ready, sig_f, gate_lin, gate_f, log_f, b_ready = map(
            sem, ("qT_ready", "sig_f", "gate_lin", "gate_f", "log_f", "b_ready"))
        arg_ready, dec_ready, qk_ready = map(sem, ("arg_ready", "dec_ready", "qk_ready"))
        arg_part = sem("arg_part")
        sc_zero, sc_ready, scX_ready = map(sem, ("sc_zero", "sc_ready", "scX_ready"))
        v_ready, g_sig, g_ready = map(sem, ("v_ready", "g_sig", "g_ready"))
        o_ready, o_sq, o_sum, o_ms, o_root, o_rstd, o_gated, o_normed = map(
            sem, ("o_ready", "o_sq", "o_sum", "o_ms", "o_root", "o_rstd", "o_gated", "o_normed"))
        obT_hi_ready, obT_ready = map(sem, ("obT_hi_ready", "obT_ready"))
        dT_ready, yaT_hi_ready, yaT_ready = map(sem, ("dT_ready", "yaT_hi_ready", "yaT_ready"))
        gates_ready, gated, m_ready, mT_hi_ready, mT_ready = map(
            sem, ("gates_ready", "gated", "m_ready", "mT_hi_ready", "mT_ready"))
        x_new, sq_ready, ms_sum, ms_ready, root_ready, rstd_ready = map(
            sem, ("x_new", "sq_ready", "ms_sum", "ms_ready", "root_ready", "rstd_ready"))
        z_ready, conv0, conv1, conv2, sig_u, prod_u, act_ready, aT_hi_ready, aT_ready = map(
            sem, ("z_ready", "conv0", "conv1", "conv2", "sig_u", "prod_u", "act_ready", "aT_hi_ready", "aT_ready"))
        pT_hi_ready, pT_ready, ple_ready, sig_ready, emb_ready, y_pre = map(
            sem, ("pT_hi_ready", "pT_ready", "ple_ready", "sig_ready", "emb_ready", "y_pre"))
        y_ready = [sem(f"y_ready{tb}") for tb in range(TB)]
        newton = sem("newton")

        def row_tiles(w):
            return w[0].rearrange("(k p) n -> p k n", p=P)

        w_in_v, w_a_v, w_b_v, w_out_v = map(row_tiles, (w_in, w_branch_a, w_branch_b, w_out))
        w_up_v, w_down_v, w_pg_v, w_ple_v = map(row_tiles, (w_up, w_down, w_ple_gate, w_ple))

        def aux_flat(name):
            return aux[:, AUX[name] % 2, :]

        def aux_blocks(name, n=4):
            return aux[:, AUX[name] % 2, 0:n * SEQ].rearrange("p (b t) -> p b t", t=SEQ)

        def aux_arrived(eng, name, it=None):
            eng.wait_ge(aux_ready, plus(AUX[name] + 1, 2, it))

        def chunk_done(eng, c, it=None):
            eng.wait_ge(units_done, plus(chunk_end(c), 2 * UK, it))

        def main_acc(c, tb, width=NCOL):
            return main[:, c % 2, tb, 0:width]

        def width_of(u, it):
            return 2 * LAST_FW if it is None and DOWN - UK + LEAD <= u < DOWN else NCOL

        def cols(n):
            return slice(n * NCOL, (n + 1) * NCOL)

        def halves(ap, m):
            return ap.rearrange("p (n a m) -> p n a m", a=2, m=m)

        bT_flat = bT[:].rearrange("p h t -> p (h t)")
        kT_flat = kT[:].rearrange("p h t -> p (h t)")
        qT_flat = qT[:].rearrange("p h t -> p (h t)")
        o_heads = dec[:, 0, :].rearrange("p (b n) -> p b n", b=TB)

        block = ctx.enter_context(nc.Block())

        @block.sync
        def _(sp):
            def slot_split(u, it=None):
                if u >= RING:
                    sp.wait_ge(lo_full, plus(u - RING + 1, 2 * UK, it))

            def rows(u, w, k, col):
                slot_split(u)
                n = min(2, w.shape[1] - k)
                sp.dma_start(raw[:, u % RING, 0:n, :], w[:, k:k + n, col:col + NCOL]).then_inc(raw_full[u % RING], 32)

            def up_unit(u, k, col, width, it=None):
                def src(c):
                    at = slice(c, c + width) if it is None else bass.ds(it * (2 * FW) + c, width)
                    return w_up_v[:, k:k + 2, at]
                slot_split(u, it)
                sp.dma_start(raw[:, u % RING, :, 0:width], src(col)).then_inc(raw_full[u % RING], 16)
                sp.dma_start(raw[:, u % RING, :, width:2 * width], src(D_FF + col)).then_inc(raw_full[u % RING], 16)

            x_v = x[0].rearrange("(b p) n -> p b n", p=P)
            sp.dma_start(mrows[:], ln_mix_w[0].rearrange("(r c) -> r c", c=P)).then_inc(const_in, 16)
            sp.dma_start(ident[:], ident_c).then_inc(const_in, 16)
            sp.dma_start(x_tok[:, :, cols(0)], x_v[:, :, cols(0)]).then_inc(x_in[0], 16)
            for u in range(4):
                rows(u, w_in_v, 2 * u, PROJ[0])
                if u < NQ - 1:
                    sp.dma_start(x_tok[:, :, cols(u + 1)], x_v[:, :, cols(u + 1)]).then_inc(x_in[u + 1], 16)
            for u in range(4, MIX):
                rows(u, w_in_v, 2 * (u % UK), PROJ[u // UK])
                if u == 14:
                    sp.dma_start(levels[:], levels_c).then_inc(late_in, 16)
                    sp.dma_start(band[:], band_c).then_inc(late_in, 16)
                    sp.dma_start(mixw[:].rearrange("p g a n -> p (g a) n"),
                                 pool_mix_w[0].rearrange("g (a p) n -> p (g a) n", p=P)).then_inc(late_in, 16)
            u = MIX
            for n in range(NQ):
                for w, k, col in ((w_in_v, UK, COL_GA), (w_in_v, UK, COL_GB), (w_a_v, UB, 0), (w_b_v, UB, 0)):
                    for i in range(k):
                        rows(u, w, 2 * i, col + n * NCOL)
                        u += 1
            for n in range(NQ):
                for i in range(UK):
                    rows(u, w_out_v, 2 * i, n * NCOL)
                    u += 1
            for i in range(UK):
                up_unit(UP + i, 2 * i, 0, FW)
            with sp.Fori(0, UP_PAIRS) as it:
                for j in (1, 2):
                    for i in range(UK):
                        up_unit(UP + j * UK + i, 2 * i, j * FW, FW, it)
            for i in range(UK):
                up_unit(DOWN - UK + i, 2 * i, (NUP - 1) * FW, LAST_FW)
            u = DOWN
            for n in range(NQ):
                for i in range(UD):
                    rows(u, w_down_v, 2 * i, n * NCOL)
                    u += 1
                    if n == 0 and i == 10:
                        sp.wait_ge(aT_ready, NUP)
                        sp.dma_start(p_tok[:], p[0, 0].rearrange("(b p) n -> p b n", p=P)).then_inc(p_in, 16)
            for n in range(NQ):
                rows(u, w_ple_v, 0, n * NCOL)
                u += 1
            for n in range(NQ):
                for i in range(UK):
                    rows(u, w_pg_v, 2 * i, n * NCOL)
                    u += 1
                    if n == 0 and i == 0:
                        sp.wait_ge(units_done, PLEW)
                        sp.dma_start(lnf[:], ln_final_w.rearrange("(a n) -> a n", a=1).to_broadcast([P, D])).then_inc(lnf_in, 16)
            out_v = out[0].rearrange("(b p) n -> p b n", p=P)
            for k in range(2):
                for tb in range(TB):
                    sp.wait_ge(y_ready[tb], k + 1)
                    half = slice(k * (D // 2), (k + 1) * (D // 2))
                    sp.dma_start(out_v[:, tb, half], x_tok[:, tb, half]).then_inc(out_done, 16)
            sp.wait_ge(out_done, 16 * 2 * TB)

        @block.tensor
        def _(pe):
            def main_released(c):
                if c < 8:
                    g, k = c // 4, c % 4
                    pe.wait_ge((tok_ready, tok_ready, v_ready, g_ready)[k], (4 * g + 2, 4 * g + 4, 2 * g + 2, 2 * g + 2)[k])
                elif c < C_MIX:
                    pe.wait_ge(tok_ready, 8 + 2 * (c - 7))
                elif c < C_WOUT:
                    n, k = (c - C_MIX) // 4, (c - C_MIX) % 4
                    pe.wait_ge(gates_ready if k < 2 else gated, 4 * n + 2 * (k % 2 + 1))
                elif c < C_UP:
                    pe.wait_ge(x_new, 2 * (c - C_WOUT + 1))
                elif c < C_DOWN:
                    pe.wait_ge(z_ready, 2 * (c - C_UP + 1))
                elif c < C_PLEW:
                    pe.wait_ge(x_new, 2 * (NQ + c - C_DOWN + 1))
                elif c < C_GATE:
                    pe.wait_ge(ple_ready, 2 * (c - C_PLEW + 1))
                else:
                    pe.wait_ge(sig_ready, 2 * (c - C_GATE + 1))

            def aux_released(name):
                kind, g = name.rstrip("0123456789."), name.split(".")[0][-1:]
                g = int(g) if g.isdigit() else 0
                if kind == "vec":
                    pe.wait_ge(vec_ready, 1)
                elif kind == "cvec":
                    pe.wait_ge(cvec_ready, 2)
                elif kind == "xT":
                    pe.wait_ge(xT_ready, 4 * (g + 1))
                elif kind == "qT":
                    pe.wait_ge(qT_ready, g + 1)
                elif kind == "fT":
                    pe.wait_ge(sig_f, 2 * (g + 1))
                elif kind == "diag":
                    pe.wait_ge(sc_ready, 8 * g + 1)
                elif kind == "prod" and name[-1] != "8":
                    pe.wait_ge(sc_ready, 8 * g + 1 + int(name[-1]))
                elif kind == "prod":
                    pe.wait_ge(scX_ready, g + 1)
                elif kind == "pv":
                    pe.wait_ge(o_ready, g + 1)
                elif kind == "obT":
                    pe.wait_ge(obT_ready, 4 * (g + 1))
                elif kind == "band":
                    pe.wait_ge(dT_ready, g + 1)
                elif kind == "mix":
                    pe.wait_ge(yaT_ready, 4 * (g + 1))
                elif kind == "mT":
                    pe.wait_ge(mT_ready, g + 1)
                elif name[:3] == "x1T":
                    pe.wait_ge(xT_ready, 4 * (NQ + g + 1))
                elif name[:3] == "x2T":
                    pe.wait_ge(xT_ready, 4 * (2 * NQ + g + 1))
                elif kind == "zT":
                    pe.wait_ge(conv2, int(name[2:]) + 1)
                elif kind == "pT":
                    pe.wait_ge(pT_ready, 1)

            def aux_begin(name):
                if AUX[name] >= 2:
                    aux_released(AUX_USES[AUX[name] - 2][1])

            def unit(u, c, i, n, hi, lo, k, it=None, width=NCOL, tiles=2):
                pe.wait_ge(lo_full, plus(u + 1, 2 * UK, it))
                for a in range(tiles):
                    for tb in range(TB):
                        acc = main_acc(c, tb, width)
                        th = hi[:, k + a, tb * P:(tb + 1) * P]
                        tl = lo[:, k + a, tb * P:(tb + 1) * P]
                        wh = w_hi[:, u % RING, a, 0:width]
                        wl = w_lo[:, u % RING, a, 0:width]
                        first, end = i == 0 and a == 0, i == n - 1 and a == tiles - 1
                        pe.matmul(acc, th, wh, start=first, stop=False)
                        pe.matmul(acc, th, wl, start=False, stop=False)
                        mm = pe.matmul(acc, tl, wh, start=False, stop=end)
                mm.then_inc(units_done, 1)

            def chunk_unit(u, c, i, n, hi, lo, k, **more):
                if i == 0 and c >= 2:
                    main_released(c - 2)
                unit(u, c, i, n, hi, lo, k, **more)
                for name in AUX_AT.get(u, ()):
                    side(name)

            def transposes(name, src, n=4):
                dst = aux_blocks(name)
                for b in range(n):
                    for tb in range(TB):
                        mm = pe.transpose(dst[:, b, tb * P:(tb + 1) * P], src(b, tb), ident[:])
                mm.then_inc(aux_ready, 1)

            def x_block(n):
                return lambda b, tb: x_tok[:, tb, n * NCOL + b * P:n * NCOL + (b + 1) * P]

            def tok_block(t):
                return lambda b, tb: t[:, tb, b * P:(b + 1) * P]

            def vectors():
                pe.wait_ge(const_in, 16 * 2)
                pe.transpose(aux_flat("vec")[:, 0:KD], mrows[:], ident[0:KD, 0:KD]).then_inc(aux_ready, 1)

            def other_vectors():
                pe.wait_ge(vec_in, 16 * 9)
                flat = aux_flat("cvec")
                pe.transpose(flat[:, NCOL:NCOL + NVEC - KD], vrows[:], ident[0:NVEC - KD, 0:NVEC - KD])
                for j in range(4):
                    o = j * P
                    mm = pe.transpose(flat[:, o:o + 2 * KF], crows[:, j, :], ident[0:2 * KF, 0:2 * KF])
                mm.then_inc(aux_ready, 1)

            def score_diag(g):
                pe.wait_ge(qT_ready, g + 1)
                pe.wait_ge(gate_f, g + 1)
                flat = aux_flat(f"diag{g}")
                for h in range(4):
                    for t in range(TB):
                        o, s = (2 * h + t) * P, slice(t * P, (t + 1) * P)
                        mm = pe.matmul(flat[:, o:o + P], kT[:, h, s], qT[:, h, s], start=True, stop=True)
                mm.then_inc(aux_ready, 1)

            def score_level(g, l):
                pe.wait_ge(qk_ready, 8 * g + l)
                flat, e = aux_flat(f"prod{g}.{l}"), dec[:, l % 2, :]
                for h in range(4):
                    for t in range(TB if l < 8 else 1):
                        a = h * SEQ + t * P
                        if l < 8:
                            o, n = (2 * h + t) * (P // 2), P // 2
                            right = halves(e[:, a:a + P], HALVES[l - 1])[:, :, 1, :]
                        else:
                            o, n, right = h * P, P, e[:, a + P:a + 2 * P]
                        mm = pe.matmul(flat[:, o:o + n], e[:, a:a + P], right, start=True, stop=True)
                mm.then_inc(aux_ready, 1)

            def read_out(g):
                pe.wait_ge(sc_ready, 8 * (g + 1))
                pe.wait_ge(scX_ready, g + 1)
                pe.wait_ge(v_ready, 2 * (g + 1))
                flat = aux_flat(f"pv{g}")
                for h in range(4):
                    hc = slice(h * P, (h + 1) * P)
                    pe.matmul(flat[:, hc], scT[:, 2 * h, :], v_tok[:, 0, hc], start=True, stop=True)
                    o = flat[:, NCOL + h * P:NCOL + (h + 1) * P]
                    pe.matmul(o, scX[:, h, :], v_tok[:, 0, hc], start=True, stop=False)
                    mm = pe.matmul(o, scT[:, 2 * h + 1, :], v_tok[:, 1, hc], start=False, stop=True)
                mm.then_inc(aux_ready, 1)

            def pool_means(g):
                pe.wait_ge(tok_ready, 8 + 2 * (g + 1))
                pe.wait_ge(late_in, 16 * 3)
                dst = aux_blocks(f"band{g}")
                for b in range(4):
                    w, bc = 2 * g + b // 2, slice(b * P, (b + 1) * P)
                    pe.matmul(dst[:, b, :], tok[:, 0, bc], band[:, w, 0:2 * P], start=True, stop=False)
                    mm = pe.matmul(dst[:, b, P:2 * P], tok[:, 1, bc], band[:, w, 2 * P:3 * P], start=False, stop=True)
                mm.then_inc(aux_ready, 1)

            def pool_mix(g):
                pe.wait_ge(dT_ready, g + 1)
                dst = aux_blocks(f"mix{g}")
                for b in range(4):
                    w, o = 2 * g + b // 2, (b % 2) * P
                    for a in range(2):
                        mm = pe.matmul(dst[:, b, :], mixw[:, w, a, o:o + P], dT[:, 2 * (b // 2) + a, :],
                                       start=(a == 0), stop=(a == 1))
                mm.then_inc(aux_ready, 1)

            def side(name):
                aux_begin(name)
                if name == "vec":
                    vectors()
                elif name == "cvec":
                    other_vectors()
                elif name[:2] == "xT":
                    pe.wait_ge(x_in[int(name[2])], 16)
                    transposes(name, x_block(int(name[2])))
                elif name[:2] == "qT":
                    pe.wait_ge(tok_ready, 4 * int(name[2]) + 2)
                    transposes(name, tok_block(tok))
                elif name[:2] == "fT":
                    pe.wait_ge(tok_ready, 4 * int(name[2]) + 4)
                    transposes(name, tok_block(tok))
                elif name[:4] == "diag":
                    score_diag(int(name[4]))
                elif name[:4] == "prod":
                    score_level(int(name[4]), int(name[6]))
                elif name[:2] == "pv":
                    read_out(int(name[2]))
                elif name[:3] == "obT":
                    pe.wait_ge(o_normed, int(name[3]) + 1)
                    transposes(name, tok_block(o_heads))
                elif name[:4] == "band":
                    pool_means(int(name[4]))
                elif name[:3] == "mix":
                    pool_mix(int(name[3]))
                elif name[:2] == "mT":
                    pe.wait_ge(m_ready, int(name[2]) + 1)
                    transposes(name, tok_block(m_tok))
                elif name[:3] == "x1T":
                    pe.wait_ge(x_new, 2 * (int(name[3]) + 1))
                    transposes(name, x_block(int(name[3])))
                elif name[:3] == "x2T":
                    pe.wait_ge(x_new, 2 * (NQ + int(name[3]) + 1))
                    transposes(name, x_block(int(name[3])))
                elif name[:2] == "zT":
                    pe.wait_ge(z_ready, 2 * (int(name[2:]) + 1))
                    transposes(name, tok_block(z_tok), n=4 if int(name[2:]) < NUP - 1 else 2)
                else:
                    pe.wait_ge(p_in, 16)
                    transposes(name, tok_block(p_tok), n=2)

            for s in (-2, -1):
                for name in AUX_AT[s]:
                    side(name)
            u = 0
            for c in range(C_MIX):
                for i in range(UK):
                    if c == 0 and i % 2 == 0:
                        pe.wait_ge(xT_ready, 4 * (i // 2 + 1))
                    chunk_unit(u, c, i, UK, xT_hi, xT_lo, 2 * i)
                    u += 1
            for n in range(NQ):
                for k, (hi, lo, nu) in enumerate(((xT_hi, xT_lo, UK), (xT_hi, xT_lo, UK),
                                                  (yaT_hi, yaT_lo, UB), (obT_hi, obT_lo, UB))):
                    for i in range(nu):
                        if n == 0 and i == 0 and k >= 2:
                            pe.wait_ge((yaT_ready, obT_ready)[k - 2], 8)
                        chunk_unit(u, C_MIX + 4 * n + k, i, nu, hi, lo, 2 * i)
                        u += 1
            for n in range(NQ):
                for i in range(UK):
                    if n == 0 and i % 2 == 0:
                        pe.wait_ge(mT_ready, i // 2 + 1)
                    chunk_unit(u, C_WOUT + n, i, UK, mT_hi, mT_lo, 2 * i)
                    u += 1
            for i in range(UK):
                if i % 2 == 0:
                    pe.wait_ge(xT_ready, 4 * (NQ + i // 2 + 1))
                chunk_unit(UP + i, C_UP, i, UK, xT_hi, xT_lo, 2 * i)
            with pe.Fori(0, UP_PAIRS) as it:
                for j in (1, 2):
                    for i in range(UK):
                        unit(UP + j * UK + i, C_UP + j, i, UK, xT_hi, xT_lo, 2 * i, it=it)
                        if i == 1:
                            pe.wait_ge(z_ready, plus(2 * j, 4, it))
                            transposes(f"zT{j - 1:02d}", tok_block(z_tok))
            for i in range(UK):
                chunk_unit(DOWN - UK + i, C_DOWN - 1, i, UK, xT_hi, xT_lo, 2 * i, width=2 * (LAST_FW))
            u = DOWN
            for n in range(NQ):
                for i in range(UD):
                    if n == 0:
                        pe.wait_ge(aT_ready, i + 1)
                    chunk_unit(u, C_DOWN + n, i, UD, aT_hi, aT_lo, 2 * i, tiles=min(2, KF - 2 * i))
                    u += 1
            for n in range(NQ):
                if n == 0:
                    pe.wait_ge(pT_ready, 1)
                chunk_unit(u, C_PLEW + n, 0, 1, pT_hi, pT_lo, 0)
                u += 1
            for n in range(NQ):
                for i in range(UK):
                    if n == 0 and i % 2 == 0:
                        pe.wait_ge(xT_ready, 4 * (2 * NQ + i // 2 + 1))
                    chunk_unit(u, C_GATE + n, i, UK, xT_hi, xT_lo, 2 * i)
                    u += 1

        @block.scalar
        def _(ac):
            def split_hi(u, it=None):
                if u >= UNITS:
                    return
                ac.wait_ge(raw_full[u % RING], plus(32 * (u // RING + 1), 32 * (2 * UK // RING), it))
                if u >= RING:
                    ac.wait_ge(units_done, plus(u - RING + 1, 2 * UK, it))
                w = width_of(u, it)
                ac.activation(w_hi[:, u % RING, :, 0:w], raw[:, u % RING, :, 0:w], ACT.Copy).then_inc(hi_full, 1)

            def store(c, dst, norm, done, func=ACT.Copy):
                chunk_done(ac, c)
                ac.wait_ge(rstd_ready, norm + 1)
                for tb in range(TB):
                    ac.activation(dst(tb), main_acc(c, tb), func, scale=rstd[:, norm, tb:tb + 1]).then_inc(done, 1)

            def hi_blocks(name, dst, first, vec, done):
                aux_arrived(ac, name)
                for b in range(4):
                    ac.activation(dst[:, first + b, :], aux_blocks(name)[:, b, :], ACT.Copy,
                                  scale=vecT[:, vec + b:vec + b + 1]).then_inc(done, 1)

            def squares(norm, n):
                for tb in range(TB):
                    if norm or n or tb:
                        ac.wait_ge(sq_ready, TB * (NQ * norm + n) + tb)
                    ac.activation(junk[:], x_tok[:, tb, cols(n)], ACT.Square,
                                  accum_out=ssq[:, norm, tb, n:n + 1]).then_inc(sq_ready, 1)

            def decay(g, l):
                ac.wait_ge(arg_ready, 8 * g + l)
                e = dec[:, l % 2, :]
                if l == 1:
                    ac.activation(halves(e, CHUNK)[:, :, 0, :], halves(e, CHUNK)[:, :, 0, :], ACT.Exp)
                    ac.activation(halves(e, CHUNK)[:, :, 1, :], halves(bT_flat, CHUNK)[:, :, 1, :],
                                  ACT.Exp).then_inc(dec_ready, 1)
                elif l < 8:
                    ac.activation(e, e, ACT.Exp).then_inc(dec_ready, 1)
                else:
                    ev = e.rearrange("p (h c m) -> p h c m", h=4, m=CHUNK)
                    bv = bT[:].rearrange("p h (c m) -> p h c m", m=CHUNK)
                    ac.activation(ev[:, :, 0:2, :], ev[:, :, 0:2, :], ACT.Exp)
                    ac.activation(ev[:, :, 2, :], bv[:, :, 2, :], ACT.Exp)
                    ac.activation(ev[:, :, 3, :], ev[:, :, 3, :], ACT.Exp).then_inc(dec_ready, 1)

            def hgrn(g, s):
                c = 4 * g
                if s == END[c]:
                    if g:
                        aux_arrived(ac, "fT0")
                    store(c, lambda tb: tok[:, tb, :], 0, tok_ready)
                if s == END[c] + 2:
                    aux_arrived(ac, f"qT{g}")
                    if g:
                        ac.wait_ge(qk_ready, 8)
                    ac.activation(qT[:], aux_blocks(f"qT{g}"), ACT.Copy).then_inc(qT_ready, 1)
                if s == END[c + 1]:
                    aux_arrived(ac, f"qT{g}")
                    store(c + 1, lambda tb: tok[:, tb, :], 0, tok_ready)
                if s == END[c + 1] + 2:
                    aux_arrived(ac, f"fT{g}")
                    ac.activation(kT[:], aux_blocks(f"fT{g}"), ACT.Sigmoid, scale=-1.0).then_inc(sig_f, 1)
                    ac.activation(bT[:], aux_blocks(f"fT{g}"), ACT.Sigmoid).then_inc(sig_f, 1)
                if s == END[c + 1] + 3:
                    ac.wait_ge(gate_f, g + 1)
                    ac.activation(bT[:], bT[:], ACT.Ln).then_inc(log_f, 1)
                if s == END[c + 2]:
                    if g:
                        aux_arrived(ac, "pv0")
                    store(c + 2, lambda tb: v_tok[:, tb, :], 0, v_ready)
                if s == END[c + 3]:
                    if g:
                        ac.wait_ge(o_gated, 1)
                    store(c + 3, lambda tb: g_tok[:, tb, :], 0, g_sig, ACT.Sigmoid)
                for l in range(1, 9):
                    if s == level_slot(g, l):
                        decay(g, l)
                if s == level_slot(g, 8) + 3:
                    aux_arrived(ac, f"prod{g}.8")
                    src = aux_flat(f"prod{g}.8")[:, 0:NCOL].rearrange("p (h t) -> p h t", h=4)
                    ac.activation(scX[:], src, ACT.Copy).then_inc(scX_ready, 1)
                if s == PV[g] + 1:
                    aux_arrived(ac, f"pv{g}")
                    ac.activation(dec[:, 0, :], aux_flat(f"pv{g}"), ACT.Copy).then_inc(o_ready, 1)

            def pool_branch(g, s):
                if s == END[8 + g]:
                    aux_arrived(ac, ("fT1", "band0")[g])
                    store(8 + g, lambda tb: tok[:, tb, :], 0, tok_ready)
                if s == END[8 + g] + 2:
                    aux_arrived(ac, f"band{g}")
                    if g:
                        aux_arrived(ac, "mix0")
                    ac.activation(dT[:], aux_blocks(f"band{g}"), ACT.Copy).then_inc(dT_ready, 1)

            def up_post(j, i, it=None):
                nf = 2 if j < NUP - 1 else 1
                f0 = lambda f: slice(f, f + 1) if it is None else bass.ds(it * 4 + f, 1)
                if i == 0:
                    chunk_done(ac, C_UP + j, it)
                    for tb in range(TB):
                        ac.activation(z_tok[:, tb, 0:2 * nf * P], main_acc(C_UP + j, tb, 2 * nf * P), ACT.Copy,
                                      scale=rstd[:, 1, tb:tb + 1]).then_inc(z_ready, 1)
                if i == 2:
                    name = f"zT{j:02d}"
                    aux_arrived(ac, name, it)
                    for b in range(2 * nf):
                        f = 2 * j + b % nf + KF * (b // nf)
                        last_op = ac.activation(cv[:, b, :], aux_blocks(name)[:, b, :], ACT.Identity,
                                                scale=convT[:, 2, f0(f)], bias=convT[:, 3, f0(f)])
                    last_op.then_inc(conv0, 1)
                if i == 4:
                    ac.wait_ge(conv2, plus(j + 1, 2, it))
                    ac.activation(act_sig[:, 0:nf, :], cv[:, 0:nf, :], ACT.Sigmoid).then_inc(sig_u, 1)
                if i == 6:
                    ac.wait_ge(act_ready, plus(j + 1, 2, it))
                    k = slice(2 * j, 2 * j + nf) if it is None else bass.ds(it * 4 + 2 * j, nf)
                    ac.activation(aT_hi[:, k, :], act[:, 0:nf, :], ACT.Copy).then_inc(aT_hi_ready, 1)

            def slot(s):
                split_hi(s + LEAD)
                if s in (0, 2, 4):
                    n = s // 2 + 1
                    hi_blocks(f"xT{n}", xT_hi, 4 * n, VCOL["ln_mix"] + 4 * n, xT_hi_ready)
                if s == 9:
                    ac.wait_ge(lb_ready, 1)
                    ac.activation(lbT[:, 0, :], lbT[:, 1, :], ACT.Sigmoid).then_inc(lb_ready, 1)
                if 3 <= s < 3 + NQ:
                    squares(0, s - 3)
                for g in range(2):
                    hgrn(g, s)
                    pool_branch(g, s)
                    if s == END[8 + g] + 4:
                        hi_blocks(f"mix{g}", yaT_hi, 4 * g, VCOL["pool_scale"] + 4 * g, yaT_hi_ready)
                    if s == OBT[g] + 1:
                        hi_blocks(f"obT{g}", obT_hi, 4 * g, VCOL["hgrn_norm"] + 4 * g, obT_hi_ready)
                for n in range(NQ):
                    if s == merge_slot(n, 0):
                        if n:
                            ac.wait_ge(m_ready, n)
                        store(C_MIX + 4 * n, lambda tb: sig_a[:, tb, :], 0, gates_ready, ACT.Sigmoid)
                    if s == merge_slot(n, 1):
                        store(C_MIX + 4 * n + 1, lambda tb: sig_b[:, tb, :], 0, gates_ready, ACT.Sigmoid)
                    if s == merge_slot(n, 3) + 2:
                        aux_arrived(ac, f"mT{n}")
                        ac.activation(mT_hi[:, 4 * n:4 * n + 4, :], aux_blocks(f"mT{n}"), ACT.Copy).then_inc(mT_hi_ready, 1)
                    for norm, at, name, vec in ((1, out_slot(n), f"x1T{n}", "ln_ffn"), (2, down_slot(n), f"x2T{n}", "ln_ple")):
                        if s == at + 1:
                            ac.wait_ge(x_new, 2 * (NQ * (norm - 1) + n + 1))
                            squares(norm, n)
                        if s == at + 2:
                            hi_blocks(name, xT_hi, 4 * n, VCOL[vec] + 4 * n, xT_hi_ready)
                    if s == ple_slot(n):
                        chunk_done(ac, C_PLEW + n)
                        for tb in range(TB):
                            ac.activation(ple_tok[:, tb, cols(n)], main_acc(C_PLEW + n, tb), ACT.Copy).then_inc(ple_ready, 1)
                    if s == gate_slot(n):
                        if n:
                            ac.wait_ge(x_new, 2 * (2 * NQ + n))
                        store(C_GATE + n, lambda tb: sig_g[:, tb, :], 2, sig_ready, ACT.Sigmoid)
                    if s == gate_slot(n) + (n < NQ - 1):
                        ac.wait_ge(x_new, 2 * (2 * NQ + n + 1))
                        squares(3, n)
                if UP + UK <= s < DOWN + UK:
                    up_post((s - UP) // UK - 1, s % UK)
                if s == P_T + 1:
                    aux_arrived(ac, "pT")
                    ac.activation(pT_hi[:], aux_blocks("pT", 2), ACT.Copy).then_inc(pT_hi_ready, 1)

            ac.wait_ge(half_set, 1)
            ac.activation(warm[:], minus_half[:], ACT.Sigmoid)
            ac.wait_ge(vec_ready, 1)
            hi_blocks("xT0", xT_hi, 0, VCOL["ln_mix"], xT_hi_ready)
            for u in range(LEAD):
                split_hi(u)
            for s in range(UP + UK):
                slot(s)
            ac.wait_ge(rstd_ready, 2)
            ac.wait_ge(cvec_ready, 2)
            with ac.Fori(0, UP_PAIRS) as it:
                for j in (1, 2):
                    for i in range(UK):
                        split_hi(UP + j * UK + i + LEAD, it)
                        up_post(j - 1, i, it)
            for s in range(DOWN - UK, UNITS + 1):
                slot(s)
            ac.wait_ge(rstd_ready, 4)
            ac.wait_ge(y_pre, TB * NQ)
            for k in range(2):
                half = x_tok[:, 1, k * (D // 2):(k + 1) * (D // 2)]
                ac.activation(half, half, ACT.Copy, scale=rstd[:, 3, 1:2]).then_inc(y_ready[1], 1)

        @block.vector
        def _(dve):
            def split_lo(u, it=None):
                if u >= UNITS:
                    return
                dve.wait_ge(hi_full, plus(u + 1, 2 * UK, it))
                w = width_of(u, it)
                dve.tensor_tensor(w_lo[:, u % RING, :, 0:w], raw[:, u % RING, :, 0:w], w_hi[:, u % RING, :, 0:w].bitcast(F32),
                                  ALU.subtract).then_inc(lo_full, 1)

            def lo_blocks(name, lo, hi, first, vec, hi_done, done, count):
                for b in range(4):
                    dve.wait_ge(hi_done, count + 2 * (b // 2) + 2)
                    dve.scalar_tensor_tensor(out=lo[:, first + b, :], in0=aux_blocks(name)[:, b, :],
                                             scalar=vecT[:, vec + b:vec + b + 1], in1=hi[:, first + b, :].bitcast(F32),
                                             op0=ALU.mult, op1=ALU.subtract).then_inc(done, 1)

            steps = [0]

            def step(ins):
                steps[0] += 1
                ins.then_inc(newton, 1)
                dve.wait_ge(newton, steps[0])

            def rsqrt(ms, first, tmp, dst, done):
                step(dve.tensor_tensor(tmp, first, first, ALU.mult))
                step(dve.scalar_tensor_tensor(out=tmp, in0=tmp, scalar=-0.5, in1=ms, op0=ALU.mult, op1=ALU.mult))
                dve.scalar_tensor_tensor(out=dst, in0=tmp, scalar=1.5, in1=first, op0=ALU.add, op1=ALU.mult).then_inc(done, 1)

            def mean_square(norm):
                dve.wait_ge(sq_ready, TB * NQ * (norm + 1))
                dve.reduce_sum(st[:, 2, :], ssq[:, norm], AX_X).then_inc(ms_sum, 1)
                dve.wait_ge(ms_sum, norm + 1)
                dve.tensor_scalar(st[:, 1, :], st[:, 2, :], 1.0 / D, EPS, ALU.mult, ALU.add).then_inc(ms_ready, 1)

            def inverse_rms(norm):
                dve.wait_ge(root_ready, norm + 1)
                rsqrt(st[:, 1, :], st[:, 0, :], st[:, 3, :], rstd[:, norm, :], rstd_ready)

            def exponents(g, l):
                prev = f"prod{g}.{l - 2}" if l > 2 else ("obT0" if g else None)
                if prev:
                    aux_arrived(dve, prev)
                e = dec[:, l % 2, :]
                if l == 1:
                    ev, bv = halves(e, CHUNK), halves(bT_flat, CHUNK)
                    end = bv[:, :, 0, CHUNK - 1:CHUNK].to_broadcast([P, 8, CHUNK])
                    dve.tensor_tensor(ev[:, :, 0, :], end, bv[:, :, 0, :], ALU.subtract).then_inc(arg_ready, 1)
                elif l < 8:
                    m = HALVES[l - 1]
                    ev, bv = halves(e, m), halves(bT_flat, m)
                    ref = bv[:, :, 0, m - 1:m].to_broadcast([P, 4 * SEQ // (2 * m), m])
                    dve.tensor_tensor(ev[:, :, 0, :], ref, bv[:, :, 0, :], ALU.subtract)
                    dve.tensor_tensor(ev[:, :, 1, :], bv[:, :, 1, :], ref, ALU.subtract).then_inc(arg_ready, 1)
                else:
                    ev = e.rearrange("p (h c m) -> p h c m", h=4, m=CHUNK)
                    bv = bT[:].rearrange("p h (c m) -> p h c m", m=CHUNK)
                    for c in range(2):
                        end = bv[:, :, c, CHUNK - 1:CHUNK].to_broadcast([P, 4, CHUNK])
                        last_op = dve.tensor_tensor(ev[:, :, c, :], end, bv[:, :, c, :], ALU.subtract)
                    last_op.then_inc(arg_part, 1)
                    dve.wait_ge(arg_part, g + 1)
                    end1 = bv[:, :, 1, CHUNK - 1:CHUNK].to_broadcast([P, 4, CHUNK])
                    end2 = bv[:, :, 2, CHUNK - 1:CHUNK].to_broadcast([P, 4, CHUNK])
                    dve.tensor_tensor(ev[:, :, 0, :], ev[:, :, 0, :], end1, ALU.add)
                    dve.tensor_tensor(ev[:, :, 3, :], bv[:, :, 3, :], end2, ALU.add).then_inc(arg_ready, 1)

            def pick(g, name, l):
                aux_arrived(dve, name)
                if l == 0:
                    dve.wait_ge(sc_zero, g + 1)
                    dve.wait_ge(late_in, 16 * 3)
                else:
                    dve.wait_ge(sc_ready, 8 * g + l)
                if l == 0:
                    dve.copy_predicated(scT[:], ident[:].rearrange("p (a t) -> p a t", a=1).bitcast(I32).to_broadcast([P, 8, P]),
                                        aux_flat(name).rearrange("p (b t) -> p b t", t=P)).then_inc(sc_ready, 1)
                    return
                m = HALVES[l - 1]
                shape = [P, 8, P // 2 // m, m]
                right = scT[:].rearrange("p b (n a m) -> p b n a m", a=2, m=m)[:, :, :, 1, :]
                mask = levels[:, l - 1, :].rearrange("p (b n m) -> p b n m", b=1, m=m).bitcast(I32).to_broadcast(shape)
                data = aux_flat(name)[:, 0:NCOL].rearrange("p (b n m) -> p b n m", b=8, m=m)
                dve.copy_predicated(right, mask, data).then_inc(sc_ready, 1)

            def hgrn(g, s):
                c = 4 * g
                if s == END[c + 1] + 2:
                    dve.wait_ge(sig_f, 2 * (g + 1))
                    for h in range(4):
                        lb, oml = (lbT[:, k, 4 * g + h:4 * g + h + 1] for k in range(2))
                        dve.tensor_scalar(kT[:, h, :], kT[:, h, :], oml, None, ALU.mult)
                        last_op = dve.tensor_scalar(bT[:, h, :], bT[:, h, :], oml, lb, ALU.mult, ALU.add)
                    last_op.then_inc(gate_lin, 1)
                    dve.wait_ge(gate_lin, g + 1)
                    dve.tensor_scalar(bT[:], bT[:], LN_MIN, None, ALU.max).then_inc(gate_f, 1)
                if s == END[c + 1] + 4:
                    dve.wait_ge(log_f, g + 1)
                    dve.wait_ge(scan_keep_set, 2)
                    dve.tensor_tensor_scan(bT_flat, scan_keep[:], bT_flat, 0.0, ALU.mult, ALU.add).then_inc(b_ready, 1)
                    dve.wait_ge(b_ready, g + 1)
                for l in range(1, 9):
                    if s == level_slot(g, l):
                        exponents(g, l)
                if s == LEVEL0[g] + 2:
                    pick(g, f"diag{g}", 0)
                for l in range(1, 8):
                    if s == level_slot(g, l) + 3:
                        pick(g, f"prod{g}.{l}", l)
                if s == END[c + 3]:
                    for tb in range(TB):
                        dve.wait_ge(g_sig, 2 * g + tb + 1)
                        dve.scalar_tensor_tensor(out=g_tok[:, tb, :], in0=main_acc(c + 3, tb), scalar=rstd[:, 0, tb:tb + 1],
                                                 in1=g_tok[:, tb, :], op0=ALU.mult, op1=ALU.mult).then_inc(g_ready, 1)
                if s == PV[g] + 1:
                    dve.wait_ge(o_ready, g + 1)
                    dve.tensor_tensor(dec[:, 1, :], dec[:, 0, :], dec[:, 0, :], ALU.mult).then_inc(o_sq, 1)
                    dve.wait_ge(o_sq, g + 1)
                    dve.reduce_sum(nrm[:, 2, :], dec[:, 1, :].rearrange("p (n v) -> p n v", v=P), AX_X).then_inc(o_sum, 1)
                    dve.wait_ge(o_sum, g + 1)
                    dve.tensor_scalar(nrm[:, 1, :], nrm[:, 2, :], 1.0 / P, EPS, ALU.mult, ALU.add).then_inc(o_ms, 1)
                if s == PV[g] + 3:
                    dve.wait_ge(o_root, g + 1)
                    rsqrt(nrm[:, 1, :], nrm[:, 0, :], nrm[:, 2, :], nrm[:, 3, :], o_rstd)
                    dve.wait_ge(o_rstd, g + 1)
                    dve.wait_ge(o_gated, g + 1)
                    ov = dec[:, 0, :].rearrange("p (n v) -> p n v", v=P)
                    dve.tensor_tensor(ov, ov, nrm[:, 3, :].rearrange("p (n a) -> p n a", a=1).to_broadcast([P, 8, P]),
                                      ALU.mult).then_inc(o_normed, 1)

            def up_post(j, i, it=None):
                nf = 2 if j < NUP - 1 else 1
                f0 = lambda f: slice(f, f + 1) if it is None else bass.ds(it * 4 + f, 1)
                if i == 2:
                    dve.wait_ge(conv0, plus(j + 1, 2, it))
                    z = aux_blocks(f"zT{j:02d}")
                    for tap, done in ((1, conv1), (0, conv2)):
                        d = 2 - tap
                        for b in range(2 * nf):
                            f = 2 * j + b % nf + KF * (b // nf)
                            last_op = dve.scalar_tensor_tensor(
                                out=cv[:, b, d:SEQ], in0=z[:, b, 0:SEQ - d], scalar=convT[:, tap, f0(f)],
                                in1=cv[:, b, d:SEQ], op0=ALU.mult, op1=ALU.add)
                        last_op.then_inc(done, 1)
                        if tap == 1:
                            dve.wait_ge(conv1, plus(j + 1, 2, it))
                if i == 4:
                    dve.wait_ge(sig_u, plus(j + 1, 2, it))
                    dve.wait_ge(prod_u, plus(j + 1, 2, it))
                    dve.tensor_tensor(act[:, 0:nf, :], act[:, 0:nf, :], act_sig[:, 0:nf, :], ALU.mult).then_inc(act_ready, 1)
                if i == 6:
                    dve.wait_ge(aT_hi_ready, plus(j + 1, 2, it))
                    k = slice(2 * j, 2 * j + nf) if it is None else bass.ds(it * 4 + 2 * j, nf)
                    dve.tensor_tensor(aT_lo[:, k, :], act[:, 0:nf, :], aT_hi[:, k, :].bitcast(F32), ALU.subtract).then_inc(aT_ready, 1)

            def slot(s):
                split_lo(s + LEAD)
                if s in (0, 2, 4):
                    n = s // 2 + 1
                    lo_blocks(f"xT{n}", xT_lo, xT_hi, 4 * n, VCOL["ln_mix"] + 4 * n, xT_hi_ready, xT_ready, 4 * n)
                if s == 6:
                    aux_arrived(dve, "cvec")
                    dve.tensor_copy(convT[:], aux_flat("cvec")[:, 0:4 * P].rearrange("p (j f) -> p j f", j=4)[:, :, 0:2 * KF]).then_inc(cvec_ready, 1)
                    dve.tensor_copy(vecT[:, KD:NVEC], aux_flat("cvec")[:, NCOL:NCOL + NVEC - KD]).then_inc(cvec_ready, 1)
                if s == 7:
                    dve.wait_ge(cvec_ready, 2)
                    lbc = VCOL["lb"]
                    dve.tensor_tensor(lbT[:, 1, :], vecT[:, lbc:lbc + 8], vecT[:, lbc + 8:lbc + 16], ALU.subtract).then_inc(lb_ready, 1)
                if s == 10:
                    dve.wait_ge(lb_ready, 2)
                    dve.tensor_scalar(lbT[:, 1, :], lbT[:, 0, :], -1.0, 1.0, ALU.mult, ALU.add).then_inc(lb_ready, 1)
                if s == UK - 1:
                    mean_square(0)
                if s == UK:
                    inverse_rms(0)
                for g in range(2):
                    hgrn(g, s)
                    if s == END[8 + g] + 4:
                        lo_blocks(f"mix{g}", yaT_lo, yaT_hi, 4 * g, VCOL["pool_scale"] + 4 * g, yaT_hi_ready, yaT_ready, 4 * g)
                    if s == OBT[g] + 1:
                        lo_blocks(f"obT{g}", obT_lo, obT_hi, 4 * g, VCOL["hgrn_norm"] + 4 * g, obT_hi_ready, obT_ready, 4 * g)
                for n in range(NQ):
                    for k, sig in ((2, sig_a), (3, sig_b)):
                        if s == merge_slot(n, k):
                            chunk_done(dve, C_MIX + 4 * n + k)
                            dve.wait_ge(gates_ready, 4 * n + 4)
                            for tb in range(TB):
                                dve.tensor_tensor(sig[:, tb, :], main_acc(C_MIX + 4 * n + k, tb), sig[:, tb, :], ALU.mult).then_inc(gated, 1)
                    if s == merge_slot(n, 3):
                        dve.wait_ge(gated, 4 * n + 4)
                        if n:
                            aux_arrived(dve, f"mT{n - 1}")
                        dve.tensor_tensor(m_tok[:], sig_a[:], sig_b[:], ALU.add).then_inc(m_ready, 1)
                    if s == merge_slot(n, 3) + 2:
                        dve.wait_ge(mT_hi_ready, n + 1)
                        dve.tensor_tensor(mT_lo[:, 4 * n:4 * n + 4, :], aux_blocks(f"mT{n}"),
                                          mT_hi[:, 4 * n:4 * n + 4, :].bitcast(F32), ALU.subtract).then_inc(mT_ready, 1)
                    for norm, c, at, name, vec in ((1, C_WOUT + n, out_slot(n), f"x1T{n}", "ln_ffn"),
                                                   (2, C_DOWN + n, down_slot(n), f"x2T{n}", "ln_ple")):
                        if s == at:
                            chunk_done(dve, c)
                            if norm == 1 and n == 0:
                                dve.wait_ge(sq_ready, TB * NQ)
                            for tb in range(TB):
                                dve.tensor_tensor(x_tok[:, tb, cols(n)], main_acc(c, tb), x_tok[:, tb, cols(n)], ALU.add).then_inc(x_new, 1)
                        if s == at + 1 and n == NQ - 1:
                            mean_square(norm)
                            inverse_rms(norm)
                        if s == at + 2:
                            lo_blocks(name, xT_lo, xT_hi, 4 * n, VCOL[vec] + 4 * n, xT_hi_ready, xT_ready, 4 * (NQ * norm + n))
                    if s == gate_slot(n):
                        dve.wait_ge(ple_ready, 2 * NQ)
                        for tb in range(TB):
                            dve.wait_ge(sig_ready, 2 * n + tb + 1)
                            dve.tensor_tensor(sig_g[:, tb, :], sig_g[:, tb, :], ple_tok[:, tb, cols(n)], ALU.mult).then_inc(emb_ready, 1)
                        for tb in range(TB):
                            dve.wait_ge(emb_ready, 2 * n + tb + 1)
                            dve.tensor_tensor(x_tok[:, tb, cols(n)], x_tok[:, tb, cols(n)], sig_g[:, tb, :], ALU.add).then_inc(x_new, 1)
                    if s == gate_slot(n) + 2 * (n < NQ - 1):
                        dve.wait_ge(lnf_in, 16)
                        for tb in range(TB):
                            dve.wait_ge(sq_ready, TB * (3 * NQ + n) + tb + 1)
                            if n == NQ - 1 and tb == 1:
                                mean_square(3)
                            dve.tensor_tensor(x_tok[:, tb, cols(n)], x_tok[:, tb, cols(n)], lnf[:, cols(n)], ALU.mult).then_inc(y_pre, 1)
                if UP + UK <= s < DOWN + UK:
                    up_post((s - UP) // UK - 1, s % UK)
                if s == P_T + 1:
                    dve.wait_ge(pT_hi_ready, 1)
                    dve.tensor_tensor(pT_lo[:], aux_blocks("pT", 2), pT_hi[:].bitcast(F32), ALU.subtract).then_inc(pT_ready, 1)

            aux_arrived(dve, "vec")
            dve.tensor_copy(vecT[:, 0:KD], aux_flat("vec")[:, 0:KD]).then_inc(vec_ready, 1)
            dve.wait_ge(vec_ready, 1)
            lo_blocks("xT0", xT_lo, xT_hi, 0, VCOL["ln_mix"], xT_hi_ready, xT_ready, 0)
            for u in range(LEAD):
                split_lo(u)
            for s in range(UP + UK):
                slot(s)
            with dve.Fori(0, UP_PAIRS) as it:
                for j in (1, 2):
                    for i in range(UK):
                        split_lo(UP + j * UK + i + LEAD, it)
                        up_post(j - 1, i, it)
            for s in range(DOWN - UK, UNITS + 1):
                slot(s)
            inverse_rms(3)
            dve.wait_ge(rstd_ready, 4)
            dve.wait_ge(y_pre, TB * NQ)
            for k in range(2):
                half = x_tok[:, 0, k * (D // 2):(k + 1) * (D // 2)]
                dve.tensor_scalar(half, half, rstd[:, 3, 0:1], None, ALU.mult).then_inc(y_ready[0], 1)

        @block.gpsimd
        def _(pool):
            def power(base, dst, done):
                pool.tensor_tensor(dst, base, minus_half[:, 0:base.shape[1]], ALU.pow).then_inc(done, 1)

            def root(norm):
                pool.wait_ge(ms_ready, norm + 1)
                power(st[:, 1, :], st[:, 0, :], root_ready)

            pool.memset(minus_half[:], -0.5).then_inc(half_set, 1)
            for src, name, n in ((ln_ffn_w, "ln_ffn", KD), (ln_ple_w, "ln_ple", KD),
                                 (pool_scale, "pool_scale", 8), (hgrn_norm_w, "hgrn_norm", 8)):
                r = VCOL[name] - KD
                pool.dma_start(vrows[r:r + n, :], src[0].rearrange("(r c) -> r c", c=P)).then_inc(vec_in, 16)
            r = VCOL["lb"] - KD
            pool.dma_start(vrows[r:r + 16, :], hgrn_lb_logits.rearrange("a (r c) -> (a r) c", c=P)).then_inc(vec_in, 16)
            for j in range(3):
                pool.dma_start(crows[:, j, :], conv_w[0, j].rearrange("(r c) -> r c", c=P)).then_inc(vec_in, 16)
            pool.dma_start(crows[:, 3, :], conv_b[0].rearrange("(r c) -> r c", c=P)).then_inc(vec_in, 16)
            pool.memset(scan_keep[:], 1.0).then_inc(scan_keep_set, 1)
            pool.wait_ge(scan_keep_set, 1)
            pool.memset(scan_keep[:].rearrange("p (n m) -> p n m", m=CHUNK)[:, :, 0:1], 0.0).then_inc(scan_keep_set, 1)
            pool.wait_ge(half_set, 1)
            root(0)
            for g in range(2):
                if g:
                    pool.wait_ge(aux_ready, AUX["pv0"] + 1)
                pool.memset(scT[:], 0.0).then_inc(sc_zero, 1)
                for l in range(1, 9):
                    pool.wait_ge(dec_ready, 8 * g + l)
                    m = HALVES[l - 1] if l < 8 else P
                    e = halves(dec[:, l % 2, :], m)
                    pool.tensor_tensor(e[:, :, 0, :], e[:, :, 0, :], halves(kT_flat, m)[:, :, 0, :], ALU.mult)
                    pool.tensor_tensor(e[:, :, 1, :], e[:, :, 1, :], halves(qT_flat, m)[:, :, 1, :], ALU.mult).then_inc(qk_ready, 1)
                pool.wait_ge(o_ms, g + 1)
                power(nrm[:, 1, :], nrm[:, 0, :], o_root)
                pool.wait_ge(g_ready, 2 * (g + 1))
                pool.tensor_tensor(dec[:, 0, :], dec[:, 0, :], g_tok[:].rearrange("p b n -> p (b n)"), ALU.mult).then_inc(o_gated, 1)

            def product(j, nf, it=None):
                pool.wait_ge(conv2, plus(j + 1, 1, it))
                pool.tensor_tensor(act[:, 0:nf, :], cv[:, 0:nf, :], cv[:, nf:2 * nf, :], ALU.mult).then_inc(prod_u, 1)

            root(1)
            with pool.Fori(0, NUP - 1) as it:
                product(0, 2, it)
            product(NUP - 1, 1)
            root(2)
            root(3)


_INS = ["x", "p", "ln_mix_w", "w_in", "pool_mix_w", "pool_scale", "hgrn_lb_logits", "hgrn_norm_w", "w_branch_a",
        "w_branch_b", "w_out", "ln_ffn_w", "w_up", "conv_w", "conv_b", "w_down", "ln_ple_w", "w_ple_gate", "w_ple",
        "ln_final_w"]


def shape_constants():
    s, t = np.arange(P)[:, None], np.arange(P)[None, :]
    masks = [((s // (2 * m) == t // (2 * m)) & (s % (2 * m) < m))[:, np.arange(P) % (2 * m) >= m] for m in HALVES]
    S, T = np.arange(SEQ)[:, None], np.arange(SEQ)[None, :]
    bands = []
    for w in WINDOWS:
        full = ((T >= S) & (T < S + w)) / np.minimum(T + 1, w) - (S == T)
        bands.append(np.concatenate([full[0:P, :], full[P:, P:]], axis=1))
    return (np.eye(P, dtype=np.float32), np.stack(masks, 1).astype(np.float32),
            np.stack(bands, 1).astype(np.float32))


def kernel(**inputs):
    import concourse.bacc as bacc
    from concourse.bass_utils import run_bass_kernel_spmd

    nc = bacc.Bacc("TRN2", target_bir_lowering=False, num_devices=1)
    arrays, args = {}, []
    constants = dict(zip(("ident_c", "levels_c", "band_c"), shape_constants()))
    for name, a in [(n, inputs[n]) for n in _INS] + list(constants.items()):
        a = np.ascontiguousarray(a)
        arrays[f"in_{name}"] = a
        args.append(nc.dram_tensor(f"in_{name}", a.shape, mybir.dt.from_np(a.dtype), kind="ExternalInput").ap())
    out = nc.dram_tensor("out_0", (1, SEQ, D), F32, kind="ExternalOutput").ap()
    build(nc, *args, out)
    r = run_bass_kernel_spmd(nc, [arrays], core_ids=[0])
    return r.results[0]["out_0"]
```
